# Optimizing a Trainium2 kernel written in Bass

```python
import jax, jax.numpy as jnp
from jax import lax
import numpy as np

D_MODEL = 1024
BATCH = 1
SEQ = 1024
DEPTH = 1
DEC_BATCH = 1
DEC_SEQ = 32
PAST_LEN = 1024

CHUNK = 64
D_MIX = D_MODEL
D_RET = D_MIX // 2
H_RET = 4
DK_RET = D_RET // H_RET
DV_RET = DK_RET
D_CONV = D_MIX - D_RET
CONV_W = 3
D_IN = 4 * D_RET + 3 * D_CONV
ROPE_THETA = 10000.0
RMS_EPS = 1e-6
PEER_HEADS = 8
N_KEYS = 128
N_EXPERTS = N_KEYS * N_KEYS
PEER_TOPK = 16
D_KEY = 256
D_KEY_HALF = D_KEY // 2
PEER_BLOCK = 256

kernel_name = "hybrid_retention_shortconv_peer_stream_step"

def rms_scale(x):
    xf = x.astype(jnp.float32)
    return xf * lax.rsqrt(jnp.mean(xf * xf, axis=-1, keepdims=True) + RMS_EPS)

def rmsnorm(x, g):
    return (rms_scale(x) * g.astype(jnp.float32)).astype(x.dtype)

def retention_log_decay():
    return np.log1p(-np.exp2(-5.0 - np.arange(H_RET))).astype(np.float32)

def rotary(x, pos):
    half = x.shape[-1] // 2
    inv = ROPE_THETA ** (-jnp.arange(half, dtype=jnp.float32) / half)
    ang = pos.astype(jnp.float32)[:, None] * inv[None, :]
    cos = jnp.cos(ang).astype(x.dtype)
    sin = jnp.sin(ang).astype(x.dtype)
    x1, x2 = x[..., :half], x[..., half:]
    return jnp.concatenate([x1 * cos - x2 * sin, x1 * sin + x2 * cos], axis=-1)

def retention_block(state, q, k, v):
    L = q.shape[2]
    lg = jnp.asarray(retention_log_decay())
    idx = jnp.arange(L, dtype=jnp.float32)
    dist = jnp.abs(idx[:, None] - idx[None, :])
    intra_decay = jnp.exp(lg[:, None, None] * dist).astype(q.dtype)
    q_decay = jnp.exp(lg[:, None] * (idx + 1.0)).astype(q.dtype)
    k_decay = jnp.exp(lg[:, None] * (L - 1.0 - idx)).astype(q.dtype)
    chunk_decay = jnp.exp(lg * L).astype(q.dtype)
    scores = jnp.einsum('bhid,bhjd->bhij', q, k) * intra_decay
    o = (jnp.einsum('bhij,bhje->bhie', scores, v)
         + jnp.einsum('bhid,bhde->bhie', q * q_decay[..., None], state))
    new_state = (chunk_decay[:, None, None] * state
                 + jnp.einsum('bhjd,bhje->bhde', k * k_decay[..., None], v))
    return o, new_state

def retention(state, q, k, v):
    B, H, L, _ = q.shape
    if L <= CHUNK:
        return retention_block(state, q, k, v)
    n = L // CHUNK

    def to_chunks(t):
        return jnp.moveaxis(t.reshape(B, H, n, CHUNK, t.shape[-1]), 2, 0)

    def step(s, qkv):
        o, s_new = retention_block(s, qkv[0], qkv[1], qkv[2])
        return s_new, o

    s_fin, o = lax.scan(step, state, (to_chunks(q), to_chunks(k), to_chunks(v)))
    o = jnp.moveaxis(o, 0, 2).reshape(B, H, L, v.shape[-1])
    return o, s_fin

def short_conv(buf, u, w):
    L = u.shape[1]
    ext = jnp.concatenate([buf.astype(u.dtype), u], axis=1)
    y = w[0] * ext[:, 0:L]
    for j in range(1, CONV_W):
        y = y + w[j] * ext[:, j:j + L]
    return y, ext[:, L:]

def peer(x, wq, keys1, keys2, u_tab, v_tab):
    shp = x.shape
    xt = x.reshape(-1, shp[-1])
    T = xt.shape[0]
    n_blk = -(-T // PEER_BLOCK)
    pad = n_blk * PEER_BLOCK - T
    xt = jnp.pad(xt, ((0, pad), (0, 0))).reshape(n_blk, PEER_BLOCK, shp[-1])

    def block(xb):
        q = (xb @ wq).reshape(PEER_BLOCK, PEER_HEADS, 2, D_KEY_HALF)
        s1 = jnp.einsum('thd,hnd->thn', q[:, :, 0], keys1)
        s2 = jnp.einsum('thd,hnd->thn', q[:, :, 1], keys2)
        v1, i1 = lax.top_k(s1, PEER_TOPK)
        v2, i2 = lax.top_k(s2, PEER_TOPK)
        cand = (v1[..., :, None] + v2[..., None, :]).reshape(PEER_BLOCK, PEER_HEADS, PEER_TOPK * PEER_TOPK)
        cidx = (i1[..., :, None] * N_KEYS + i2[..., None, :]).reshape(PEER_BLOCK, PEER_HEADS, PEER_TOPK * PEER_TOPK)
        top_s, sel = lax.top_k(cand, PEER_TOPK)
        eidx = jnp.take_along_axis(cidx, sel, axis=-1)
        gate = jax.nn.softmax(top_s.astype(jnp.float32), axis=-1).astype(xb.dtype)
        act = jax.nn.gelu(jnp.einsum('td,thkd->thk', xb, u_tab[eidx]))
        return jnp.einsum('thk,thkd->td', gate * act, v_tab[eidx])

    out = lax.map(block, xt)
    return out.reshape(-1, shp[-1])[:T].reshape(shp)

def layer(x, ret_state, conv_buf, pos0, g_mix, w_in, conv_w, w_out, g_ffn, wq, keys1, keys2, u_tab, v_tab):
    B, L, _ = x.shape
    h = rmsnorm(x, g_mix)
    proj = h @ w_in
    q, k, v, g, gb, gc, hc = jnp.split(
        proj, [D_RET, 2 * D_RET, 3 * D_RET, 4 * D_RET, 4 * D_RET + D_CONV, 4 * D_RET + 2 * D_CONV], axis=-1)

    def heads(t):
        return t.reshape(B, L, H_RET, -1).transpose(0, 2, 1, 3)

    pos = pos0 + jnp.arange(L, dtype=jnp.int32)
    q = rotary(heads(q), pos) * (DK_RET ** -0.5)
    k = rotary(heads(k), pos)
    o, ret_new = retention(ret_state, q, k, heads(v))
    o = rms_scale(o).astype(x.dtype)
    o = o.transpose(0, 2, 1, 3).reshape(B, L, D_RET) * jax.nn.silu(g)

    conv_y, conv_new = short_conv(conv_buf, gc * hc, conv_w)
    c = gb * conv_y

    x = x + jnp.concatenate([o, c], axis=-1) @ w_out
    x = x + peer(rmsnorm(x, g_ffn), wq, keys1, keys2, u_tab, v_tab)
    return x, ret_new, conv_new

def setup_inputs(seed: int = 0) -> dict:
    key = jax.random.key(seed)
    ks = jax.random.split(key, 16)
    nrm = jax.random.normal
    f32 = jnp.float32
    return {
        "x_prompt": nrm(ks[0], (BATCH, SEQ, D_MODEL), f32),
        "x_sample": nrm(ks[1], (DEC_BATCH, DEC_SEQ, D_MODEL), f32),
        "state_ret": nrm(ks[2], (DEPTH, DEC_BATCH, H_RET, DK_RET, DV_RET), f32),
        "state_conv": nrm(ks[3], (DEPTH, DEC_BATCH, CONV_W - 1, D_CONV), f32),
        "norm_mix_g": 1.0 + 0.02 * nrm(ks[4], (DEPTH, D_MODEL), f32),
        "w_in": nrm(ks[5], (DEPTH, D_MODEL, D_IN), f32) * D_MODEL ** -0.5,
        "conv_w": nrm(ks[6], (DEPTH, CONV_W, D_CONV), f32) * CONV_W ** -0.5,
        "w_out": nrm(ks[7], (DEPTH, D_MIX, D_MODEL), f32) * D_MIX ** -0.5,
        "norm_ffn_g": 1.0 + 0.02 * nrm(ks[8], (DEPTH, D_MODEL), f32),
        "peer_wq": nrm(ks[9], (DEPTH, D_MODEL, PEER_HEADS * D_KEY), f32) * D_MODEL ** -0.5,
        "peer_keys1": nrm(ks[10], (DEPTH, PEER_HEADS, N_KEYS, D_KEY_HALF), f32) * D_KEY_HALF ** -0.5,
        "peer_keys2": nrm(ks[11], (DEPTH, PEER_HEADS, N_KEYS, D_KEY_HALF), f32) * D_KEY_HALF ** -0.5,
        "peer_u": nrm(ks[12], (DEPTH, N_EXPERTS, D_MODEL), f32) * D_MODEL ** -0.5,
        "peer_v": nrm(ks[13], (DEPTH, N_EXPERTS, D_MODEL), f32) * PEER_HEADS ** -0.5,
        "norm_final_g": 1.0 + 0.02 * nrm(ks[14], (D_MODEL,), f32),
    }

def reference(x_prompt, x_sample, state_ret, state_conv, norm_mix_g, w_in, conv_w, w_out,
              norm_ffn_g, peer_wq, peer_keys1, peer_keys2, peer_u, peer_v, norm_final_g):
    yp, ys = x_prompt, x_sample
    bp = x_prompt.shape[0]
    rp_list, cp_list, rs_list, cs_list = [], [], [], []
    for l in range(DEPTH):
        w = (norm_mix_g[l], w_in[l], conv_w[l], w_out[l], norm_ffn_g[l],
             peer_wq[l], peer_keys1[l], peer_keys2[l], peer_u[l], peer_v[l])
        r0 = jnp.zeros((bp, H_RET, DK_RET, DV_RET), x_prompt.dtype)
        c0 = jnp.zeros((bp, CONV_W - 1, D_CONV), x_prompt.dtype)
        yp, rp, cp = layer(yp, r0, c0, 0, *w)
        ys, rs, cs = layer(ys, state_ret[l].astype(x_sample.dtype), state_conv[l], PAST_LEN, *w)
        rp_list.append(rp)
        cp_list.append(cp)
        rs_list.append(rs)
        cs_list.append(cs)
    y_prompt = rmsnorm(yp, norm_final_g)
    y_sample = rmsnorm(ys, norm_final_g)
    new_state_ret_prompt = jnp.stack(rp_list)
    new_state_conv_prompt = jnp.stack(cp_list)
    new_state_ret_sample = jnp.stack(rs_list)
    new_state_conv_sample = jnp.stack(cs_list)
    return (y_prompt, y_sample, new_state_ret_prompt, new_state_conv_prompt, new_state_ret_sample, new_state_conv_sample)


_drawn_inputs = setup_inputs


def setup_inputs(seed=0):
    import zlib

    import numpy as np

    out = dict(_drawn_inputs(seed))
    spreads = {}
    factors = {'norm_ffn_g': 2.89, 'norm_final_g': 2.874}
    for name, (base, spread) in spreads.items():
        noise = np.random.default_rng([zlib.crc32(name.encode()), seed]).standard_normal(out[name].shape)
        drawn = base * np.exp(spread * noise) if base else spread * noise
        out[name] = __import__('jax').numpy.asarray(drawn.astype(out[name].dtype))
    for name, factor in factors.items():
        out[name] = (out[name] * factor).astype(out[name].dtype)
    return out
```

```python
from contextlib import ExitStack

import concourse.bass as bass
from concourse import mybir

F32 = mybir.dt.float32
I32 = mybir.dt.int32
U32 = mybir.dt.uint32
ALU = mybir.AluOpType
ACT = mybir.ActivationFunctionType
AX_X = mybir.AxisListType.X

P = 128
D = 1024
KC = D // P
SEQ = 1024
DEC = 32
TOK = SEQ + DEC
TILES = SEQ // P
H = 4
RET = H * P
CH = (D - RET) // P
PH = 8
BLK = 2 * PH
NK = 128
TOPK = 16
STEPS = PH * TOPK
QUADS = P // DEC
SAMPLE_STEPS = STEPS // QUADS
RING = 8
PAIR = 2
SLOTS = STEPS // PAIR
WQ_RES = 8
WBUF = 2
STREAMED = BLK - WQ_RES
TOK_A = P
TOK_C = TOK - TOK_A
UNIT = 256
RET_UNITS = 4 * RET // UNIT
CONV_UNITS = 3 * CH
UNITS = CONV_UNITS + RET_UNITS
EPS = 1e-6
LOWEST = -3.0e38

S_ROPE, S_KDECAY, S_QKT, S_SCORES, S_DECAYED, S_OUT, S_GATED, S_GATEDT = 2, 4, 5, 6, 7, 8, 9, 12
S_WOUT = 13
S_X1, S_XN, S_XNT = 21, 22, 23
S_QUERY = 25
S_TOP = 31
S_PAIRS = 47
S_BEST = 48
S_PICK = 56


class Group:

    def __init__(self, t0, tiles, buffers, earlier=None):
        self.t0, self.tiles, self.buffers = t0, tiles, buffers
        self.sample = tiles[-1] == DEC
        self.tok = sum(tiles)
        self.prompt = self.tok - (DEC if self.sample else 0)
        self.chunks = [(lo, min(lo + 512, self.tok)) for lo in range(0, self.tok, 512)]
        self.uses = [(3 * c + part, kind, i) for c in range(CH) for part, kind in enumerate("ChB")
                     for i in range(len(self.chunks))]
        self.conv_uses = len(self.uses)
        self.uses += [(CONV_UNITS + u, "tile", i) for u in range(RET_UNITS) for i in range(len(tiles))]
        self.by_act = [kind in ("tile", "C") for _, kind, _ in self.uses]
        self.block_ops = 5 + 4 * self.sample
        self.per = dict(uses=len(self.uses), act=sum(self.by_act), dve=len(self.uses) - sum(self.by_act),
                        ops=CH * self.block_ops, tiles=RET_UNITS * len(tiles), blocks=CH)
        self.before = {what: earlier.before[what] + earlier.per[what] if earlier else 0 for what in self.per}
        self.loads_before = [len(range(b, UNITS, earlier.buffers)) if earlier else 0 for b in range(buffers)]
        assert self.per["uses"] % 2 == 0 and self.conv_uses % 2 == 0

    def count(self, what, n=0):
        return self.before[what] + n

    def end(self, what):
        return self.count(what, self.per[what])

    def taken(self, q):
        who = "act" if self.by_act[q] else "dve"
        return who, sum(x == self.by_act[q] for x in self.by_act[:q + 1])

    def last_use(self, unit):
        return max(q for q, use in enumerate(self.uses) if use[0] == unit)

    def slot(self, q):
        return 1 + q * (SLOTS - 2) // len(self.uses)


GROUP_A = Group(0, [P], 4)
GROUP_C = Group(1, [P] * (TILES - 1) + [DEC], 2, GROUP_A)


def layer_kernel(nc, xT, x, w_ret, w_conv, w_out, wq, keysT, uv, g_mix, g_ffn, g_fin, conv_par,
                 ret_state, cos_sin, decay_p, decay_s, edge_p, edge_s, block_decay, ident, sel, iota,
                 y, out_ret_p, out_ret_s, out_conv_p, out_conv_s):
    proj = nc.dram_tensor("proj_scratch", (TOK, 4 * RET), F32).ap()
    convT = nc.dram_tensor("conv_scratch", (CH * P, TOK), F32).ap()

    with ExitStack() as ctx:
        def sb(name, shape, dt=F32):
            return ctx.enter_context(nc.sbuf_tensor(name, shape, dt))

        def sem(name):
            return ctx.enter_context(nc.semaphore(name))

        ring = sb("ring", [P, RING, 2 * D])
        arena = sb("arena", [P, 7680])
        w_out_sb = sb("w_out_sb", [P, KC, D])
        wq_sb = sb("wq_sb", [P, WQ_RES + WBUF, KC, P])
        keys_sb = sb("keys_sb", [P, BLK, NK])
        x1_next = sb("x1_next", [P, D])
        xn_next = sb("xn_next", [P, D])
        xn_cur = sb("xn_cur", [P, D])
        g_ffn_sb = sb("g_ffn_sb", [P, D])
        g_fin_sb = sb("g_fin_sb", [P, D])
        ident_sb = sb("ident_sb", [P, P])
        sel_sb = sb("sel_sb", [P, DEC])
        iota_sb = sb("iota_sb", [P, TOPK])
        decay_p_sb = sb("decay_p_sb", [P, H, P])
        decay_s_sb = sb("decay_s_sb", [DEC, H, DEC])
        edge_p_sb = sb("edge_p_sb", [P, 2, H])
        edge_s_sb = sb("edge_s_sb", [DEC, 2, H])
        cs_sb = sb("cs_sb", [P, 2, P])
        state = sb("state", [P, H, P])
        diag = sb("diag", [P, 2, PAIR, P])
        top_v = sb("top_v", [P, BLK, TOPK])
        top_i = sb("top_i", [P, BLK, TOPK], U32)
        idx_next = sb("idx_next", [P, STEPS], I32)
        idx_cur = sb("idx_cur", [P, STEPS], I32)
        gate_next = sb("gate_next", [P, PH, TOPK])
        gate_cur = sb("gate_cur", [P, STEPS])
        dots = sb("dots", [P, STEPS])
        weights = sb("weights", [P, STEPS])
        reduced = sb("reduced", [P, 2 * PH])
        stat = sb("stat", [P, 8])
        eps_sb = sb("eps_sb", [P, 1])
        g_mix_sb = sb("g_mix_sb", [P, KC])
        par = sb("par", [P, CH, 5])
        new_tail = sb("new_tail", [P, CH, 2, 2])

        flat = ring[:, :, :].rearrange("p r d -> p (r d)")
        xn_a = flat[:, 0:KC * TOK_A].rearrange("p (k t) -> p k t", k=KC)
        xn_c = flat[:, KC * TOK_A:KC * TOK].rearrange("p (k t) -> p k t", k=KC)
        at = KC * TOK
        units = [flat[:, at:at + KC * UNIT], flat[:, at + KC * UNIT:at + 2 * KC * UNIT],
                 arena[:, 0:KC * UNIT], arena[:, KC * UNIT:2 * KC * UNIT]]
        at += 2 * KC * UNIT
        rstd_all = flat[:, at:at + TOK]
        squares = flat[:, at + TOK:at + 3 * TOK].rearrange("p (b t) -> p b t", b=2)
        gate_c = flat[:, at:at + TOK_C]
        conv_y = flat[:, at + TOK_C:at + 2 * TOK_C + 2]
        conv_out = flat[:, at + 2 * TOK_C + 2:at + 3 * TOK_C + 2]
        taps = flat[:, at + 3 * TOK_C + 2:at + 4 * TOK_C + 6]
        assert at + 4 * TOK_C + 6 <= RING * 2 * D
        ones = xn_cur[:, 0:P]
        stored = xn_cur[:, P:P + 2 * UNIT].rearrange("p (b n) -> p b n", b=2)
        wq_buf = wq_sb[:, WQ_RES:]

        qkvg = arena[:, 0:2048]
        rot = arena[:, 2048:3072].rearrange("p (g c) -> p g c", g=2 * H)
        swap = arena[:, 3072:4096].rearrange("p (g c) -> p g c", g=2 * H)
        qkT = swap
        k_dec = arena[:, 4096:4608].rearrange("p (h c) -> p h c", h=H)
        decayed = arena[:, 4608:5120].rearrange("p (h c) -> p h c", h=H)
        ret_sq = decayed
        ret_o = arena[:, 5120:5632].rearrange("p (h c) -> p h c", h=H)
        catT = arena[:, 5632:6656].rearrange("p (k c) -> p k c", k=KC)
        xnT = catT
        qT = arena[:, 6656:7680].rearrange("p (g b c) -> p g b c", g=2, b=4)
        pairs = arena[:, 0:2048].rearrange("p (h i j) -> p h i j", h=PH, i=TOPK)
        scores = arena[:, 2048:4096].rearrange("p (b n) -> p b n", b=BLK)
        onehot = arena[:, 2048:4096].rearrange("p (k j) -> p k j", j=TOPK)
        left = arena[:, 5120:5376]
        best_v = arena[:, 5376:5504].rearrange("p (h k) -> p h k", h=PH)
        best_i = arena[:, 5504:5632].bitcast(U32).rearrange("p (h k) -> p h k", h=PH)
        half_i = arena[:, 5632:5888].bitcast(U32).rearrange("p (s k) -> p s k", s=2)
        half_f = arena[:, 5888:6144].rearrange("p (s k) -> p s k", s=2)
        pick_f = arena[:, 6144:6400].rearrange("p (s k) -> p s k", s=2)
        top_f = arena[:, 6400:6656].rearrange("p (b k) -> p b k", b=BLK)
        y_sb = arena[:, 6656:7680]

        expert_sum = ctx.enter_context(nc.psum_tensor("expert_sum", [P, D], F32))
        x1_ps = ctx.enter_context(nc.psum_tensor("x1_ps", [P, D], F32))
        tp = ctx.enter_context(nc.psum_tensor("tp", [P, 2, 512], F32))
        mm = ctx.enter_context(nc.psum_tensor("mm", [P, 2, 512], F32))
        bank = [expert_sum[:, 0:512], expert_sum[:, 512:D]]
        rms_ps = [x1_ps[:, 0:512], x1_ps[:, 512:D], tp[:, 1, 0:DEC]]

        consts_in = sem("consts_in")
        eps_set = sem("eps_set")
        xT_in = sem("xT_in")
        g_mix_in = sem("g_mix_in")
        unit_in = [sem(f"unit_in{i}") for i in range(GROUP_A.buffers)]
        squared = sem("squared")
        summed = sem("summed")
        rooted = sem("rooted")
        normed = sem("normed")
        projected = sem("projected")
        act_took = sem("act_took")
        dve_took = sem("dve_took")
        stored_out = [sem("stored_out0"), sem("stored_out1")]
        par_in = sem("par_in")
        conv_ops = sem("conv_ops")
        conv_out_done = sem("conv_out_done")
        tails_out = sem("tails_out")
        inits = sem("inits")

        tile_in = sem("tile_in")
        silu_done = sem("silu_done")
        rotated = sem("rotated")
        qkT_ready = sem("qkT_ready")
        qkT_copied = sem("qkT_copied")
        scores_ready = sem("scores_ready")
        decayed_ready = sem("decayed_ready")
        ret_ready = sem("ret_ready")
        ret_squared = sem("ret_squared")
        ret_rooted = sem("ret_rooted")
        gated = sem("gated")
        gatedT_ready = sem("gatedT_ready")
        gatedT_copied = sem("gatedT_copied")
        wout_chunk = sem("wout_chunk")
        x1_ready = sem("x1_ready")
        x1_squared = sem("x1_squared")
        xn_ready = sem("xn_ready")
        xnT_ready = sem("xnT_ready")
        xnT_copied = sem("xnT_copied")
        resident_in = sem("resident_in")
        wbuf_in = [sem(f"wbuf_in{i}") for i in range(WBUF)]
        query_blk = sem("query_blk")
        query_copied = sem("query_copied")
        keyed = sem("keyed")
        keyed_copied = sem("keyed_copied")
        exp_in = sem("exp_in")
        exp_done = sem("exp_done")
        chosen = sem("chosen")
        mix_dve = sem("mix_dve")
        state_out = sem("state_out")

        landed = [sem(f"landed{i}") for i in range(RING)]
        slot_free = sem("slot_free")
        idx_copied = sem("idx_copied")
        xn_copied = sem("xn_copied")
        gate_copied = sem("gate_copied")
        dotted = sem("dotted")
        gelu_done = sem("gelu_done")
        weighed = sem("weighed")
        diag_ready = sem("diag_ready")
        sum_started = sem("sum_started")
        sum_squared = sem("sum_squared")
        sum_stat = sem("sum_stat")
        y_ready = sem("y_ready")
        y_out = sem("y_out")

        MIX_OPS = 148
        CHUNKS = [(0, 512), (512, 1024), (1024, TOK)]
        TAKEN = dict(act=act_took, dve=dve_took)

        CONSTS = [
            (g_ffn_sb[:, :], g_ffn), (g_fin_sb[:, :], g_fin),
            (ident_sb[:, :], ident), (sel_sb[:, :], sel), (iota_sb[:, :], iota),
            (decay_p_sb[:, :, :], decay_p), (decay_s_sb[:, :, :], decay_s), (edge_p_sb[:, :, :], edge_p),
            (edge_s_sb[:, :, :], edge_s), (keys_sb[:, :, :], keysT),
            (w_out_sb[:, :, :], w_out),
        ]

        pool_waited, dve_waited = sem("pool_waited"), sem("dve_waited")

        def wait(eng, s, value):
            if not isinstance(value, int) or value > 0:
                eng.wait_ge(s, value)

        def wait_apart(eng, s, value):
            if not isinstance(value, int) or value > 0:
                eng.wait_ge(s, value)
                eng.sem_inc(pool_waited if eng is nc.gpsimd else dve_waited, 1)

        def advance(program, slot):
            while program[1] <= slot:
                program[1] = next(program[0], SLOTS + 1)

        def started(generator):
            return [generator, -1]

        def together(*programs):
            programs = [started(p) for p in programs]
            for slot in range(SLOTS + 1):
                for p in programs:
                    advance(p, slot)

        def bc(ap, axis, n):
            ap = ap.unsqueeze(axis)
            shape = list(ap.shape)
            shape[axis] = n
            return ap.broadcast_to(shape)

        def projection_stored(eng, g):
            for q in stored_out:
                eng.wait_ge(q, 16 * g.end("tiles") // 2)
            eng.wait_ge(conv_out_done, 16 * g.end("blocks"))

        def unit_count(g, u):
            return 16 * (g.loads_before[u % g.buffers] + u // g.buffers + 1)

        block = ctx.enter_context(nc.Block())

        @block.sync
        def _(sp):
            sp.sem_inc(y_out, 16)
            for k in range(KC):
                sp.dma_start(xn_a[:, k, :], xT[k * P:(k + 1) * P, 0:TOK_A]).then_inc(xT_in, 16)
                sp.dma_start(xn_c[:, k, :], xT[k * P:(k + 1) * P, TOK_A:]).then_inc(xT_in, 16)
            sp.dma_start(g_mix_sb[:, :], g_mix).then_inc(g_mix_in, 16)

            def load_units(g):
                for u in range(UNITS):
                    if u >= g.buffers:
                        q = g.last_use(u - g.buffers)
                        yield g.slot(q)
                        sp.wait_ge(projected, g.count("uses", q + 1))
                    else:
                        yield 0
                        if g is GROUP_C:
                            last = max(v for v in range(UNITS) if v % GROUP_A.buffers == u)
                            sp.wait_ge(projected, GROUP_A.count("uses", GROUP_A.last_use(last) + 1))
                    dst = units[u % g.buffers]
                    if u < CONV_UNITS:
                        sp.dma_start(dst[:, 0:KC * P], w_conv[u]).then_inc(unit_in[u % g.buffers], 16)
                    else:
                        sp.dma_start(dst, w_ret[u - CONV_UNITS]).then_inc(unit_in[u % g.buffers], 16)

            def load_tile(t, n):
                rows = bass.ds(t * P, P) if n == P else bass.ds(SEQ, n)
                yield 0
                wait(sp, chosen, t)
                wait(sp, sum_started, t)
                sp.dma_start(qkvg[0:n, :], proj[rows, :]).then_inc(tile_in, 16)
                sp.dma_start(cs_sb[0:n, :, :], cos_sin[rows, :, :]).then_inc(tile_in, 16)
                sp.dma_start(x1_next[0:n, :], x[rows, :]).then_inc(tile_in, 16)
                sp.dma_start(catT[:, H:, 0:n],
                             convT[:, rows].rearrange("(c p) t -> p c t", p=P)).then_inc(tile_in, 16)
                for i in range(STREAMED):
                    if i < WBUF:
                        wait(sp, query_blk, t * BLK)
                    else:
                        b = WQ_RES + i - WBUF
                        yield S_QUERY + b
                        sp.wait_ge(query_blk, t * BLK + b + 1)
                    sp.dma_start(wq_buf[:, i % WBUF], wq[WQ_RES + i]).then_inc(wbuf_in[i % WBUF], 16)

            def store_tile(t, n):
                yield SLOTS
                sp.wait_ge(y_ready, t + 2)
                rows = bass.ds(t * P, P) if n == P else bass.ds(SEQ, n)
                sp.dma_start(y[rows, :], y_sb[0:n, :]).then_inc(y_out, 16)

            def first_tile():
                yield 0
                for dst, src in CONSTS:
                    sp.dma_start(dst, src).then_inc(consts_in, 16)
                projection_stored(sp, GROUP_A)
                sp.wait_ge(projected, GROUP_A.end("uses"))
                yield from load_tile(0, P)

            sp.dma_start(par[:, :, :], conv_par).then_inc(par_in, 16)
            together(load_units(GROUP_A))
            for i in range(WQ_RES):
                sp.dma_start(wq_sb[:, i], wq[i]).then_inc(resident_in, 16)
            together(load_units(GROUP_C), first_tile())
            sp.wait_ge(conv_ops, GROUP_C.end("ops"))
            sp.dma_start(out_conv_p, new_tail[:, :, 0, :]).then_inc(tails_out, 16)
            sp.dma_start(out_conv_s, new_tail[:, :, 1, :]).then_inc(tails_out, 16)
            projection_stored(sp, GROUP_C)
            with sp.Fori(0, TILES - 1) as t:
                together(load_tile(t + 1, P), store_tile(t, P))
            sp.wait_ge(chosen, TILES)
            sp.dma_start(out_ret_p, state[:, :, :]).then_inc(state_out, 16)
            sp.wait_ge(state_out, 16)
            sp.dma_start(state[:, :, :], ret_state).then_inc(state_out, 16)
            together(load_tile(TILES, DEC))
            sp.wait_ge(chosen, TILES + 1)
            sp.dma_start(out_ret_s, state[:, :, :]).then_inc(state_out, 16)
            together(store_tile(TILES - 1, P))
            together(store_tile(TILES, DEC))
            sp.wait_ge(state_out, 48)
            sp.wait_ge(tails_out, 32)
            sp.wait_ge(y_out, 16 * (TILES + 2))

        @block.gpsimd
        def _(pool):
            def gathers(base, ks):
                for k in ks:
                    wait_apart(pool, slot_free, base + k + 1)
                    pool.indirect_dma_start(ring[:, k % RING, :], None, uv,
                                            bass.IndirectOffsetOnAxis(ap=idx_cur[:, k:k + 1], axis=0)
                                            ).then_inc(landed[k % RING], 16)

            def take(t, i):
                half = slice(i * STEPS // 2, (i + 1) * STEPS // 2)
                pool.tensor_copy(idx_cur[:, half], idx_next[:, half]).then_inc(idx_copied, 1)
                wait_apart(pool, idx_copied, 2 * t + i + 1)

            with pool.Fori(0, TILES) as t:
                wait_apart(pool, chosen, t + 1)
                take(t, 0)
                gathers(t * STEPS, range(0, 2 * RING))
                take(t, 1)
                gathers(t * STEPS, range(2 * RING, STEPS))
            pool.wait_ge(idx_copied, 2 * TILES + QUADS)
            gathers(TILES * STEPS, range(SAMPLE_STEPS))

        @block.scalar
        def _(act):
            for k in range(KC):
                act.wait_ge(xT_in, 16 * 2 * KC)
                if k >= 2:
                    act.wait_ge(summed, k - 1)
                act.activation(squares[:, k % 2, 0:TOK_A], xn_a[:, k, :], ACT.Square).then_inc(squared, 1)
                act.activation(squares[:, k % 2, TOK_A:], xn_c[:, k, :], ACT.Square).then_inc(squared, 1)
            act.wait_ge(summed, KC)
            act.wait_ge(inits, 1)
            for (lo, hi), src in zip(CHUNKS, rms_ps):
                act.activation(rstd_all[:, lo:hi], src, ACT.Sqrt, bias=eps_sb[:, :], scale=1.0 / D).then_inc(rooted, 1)

            def projection(g):
                for q, (u, kind, i) in enumerate(g.uses):
                    if not g.by_act[q]:
                        continue
                    yield g.slot(q)
                    act.wait_ge(projected, g.count("uses", q + 1))
                    if kind == "C":
                        lo, hi = g.chunks[i]
                        if i == 0:
                            earlier = [p for p in range(q) if g.uses[p][1] == "h"]
                            wait(act, dve_took, g.count("dve", g.taken(earlier[-1])[1] if earlier else 0))
                        act.activation(gate_c[:, lo:hi], bank[q % 2][:, 0:hi - lo], ACT.Copy).then_inc(act_took, 1)
                        continue
                    m = g.tiles[i]
                    wait(act, stored_out[q % 2], 16 * ((g.count("tiles") + q - g.conv_uses) // 2))
                    act.activation(stored[0:m, q % 2, :], bank[q % 2][0:m, 0:UNIT], ACT.Copy).then_inc(act_took, 1)
                    act.wait_ge(act_took, g.count("act", g.taken(q)[1]))
                    row, col = (g.t0 + i) * P, (u - CONV_UNITS) * UNIT
                    act.dma_start(proj[row:row + m, col:col + UNIT], stored[0:m, q % 2, :]).then_inc(stored_out[q % 2], 16)

            def store_conv(g):
                for c in range(CH):
                    last = g.last_use(3 * c + 2)
                    yield g.slot(last + 2)
                    act.wait_ge(dve_took, g.count("dve", g.taken(last)[1]))
                    act.wait_ge(conv_ops, g.count("ops", (c + 1) * g.block_ops))
                    act.dma_start(convT[c * P:(c + 1) * P, g.t0 * P:g.t0 * P + g.tok],
                                  conv_out[:, 0:g.tok]).then_inc(conv_out_done, 16)

            together(projection(GROUP_A), store_conv(GROUP_A))

            def mixer(t, n):
                yield S_ROPE
                act.wait_ge(tile_in, 64 * (t + 1))
                act.activation(qkvg[0:n, 3 * RET:], qkvg[0:n, 3 * RET:], ACT.Silu).then_inc(silu_done, 1)
                yield S_QKT
                for i in range(2):
                    act.wait_ge(qkT_ready, t * 2 + i + 1)
                    act.activation(qkT[:, i * H:(i + 1) * H, 0:n],
                                   tp[:, i, :].rearrange("p (h c) -> p h c", h=H)[:, :, 0:n],
                                   ACT.Copy).then_inc(qkT_copied, 1)
                yield S_GATED + 1
                act.wait_ge(ret_squared, t + 1)
                act.activation(stat[0:n, 0:H], stat[0:n, 0:H], ACT.Sqrt, bias=eps_sb[0:n, :],
                               scale=1.0 / P).then_inc(ret_rooted, 1)
                yield S_GATEDT
                act.wait_ge(gatedT_ready, t + 1)
                act.activation(catT[:, 0:H, 0:n], mm[:, 0, :].rearrange("p (h c) -> p h c", h=H)[:, :, 0:n],
                               ACT.Copy).then_inc(gatedT_copied, 1)
                yield S_X1
                act.wait_ge(x1_ready, t + 1)
                wait(act, xn_copied, t)
                act.activation(xn_next[0:n, :], x1_next[0:n, :], ACT.Square,
                               accum_out=stat[0:n, 4:5]).then_inc(x1_squared, 1)
                act.wait_ge(x1_squared, 2 * t + 1)
                act.activation(stat[0:n, 4:5], stat[0:n, 4:5], ACT.Sqrt, bias=eps_sb[0:n, :],
                               scale=1.0 / D).then_inc(x1_squared, 1)
                yield S_XNT
                for i in range(2):
                    if i:
                        yield S_XNT + 1
                    act.wait_ge(xnT_ready, t * 2 + i + 1)
                    act.activation(xnT[:, i * 4:(i + 1) * 4, 0:n],
                                   tp[:, i, :].rearrange("p (h c) -> p h c", h=4)[:, :, 0:n],
                                   ACT.Copy).then_inc(xnT_copied, 1)
                for g in range(4):
                    yield S_QUERY + 4 * g + 3
                    act.wait_ge(query_blk, t * BLK + 4 * g + 4)
                    if g >= 2:
                        act.wait_ge(keyed, t * 4 + g - 1)
                    if g == 0:
                        wait(act, y_out, 16 * t)
                    act.activation(qT[:, g % 2, :, 0:n],
                                   mm[:, g % 2, :].rearrange("p (b c) -> p b c", b=4)[:, :, 0:n],
                                   ACT.Copy).then_inc(query_copied, 1)
                    yield S_QUERY + 4 * g + 5
                    act.wait_ge(keyed, t * 4 + g + 1)
                    act.activation(scores[0:n, 4 * g:4 * g + 4, :],
                                   tp[0:n, g % 2, :].rearrange("p (b c) -> p b c", b=4),
                                   ACT.Copy).then_inc(keyed_copied, 1)
                yield S_PICK + 1
                act.wait_ge(exp_in, t + 1)
                act.activation(gate_next[0:n], gate_next[0:n], ACT.Exp).then_inc(exp_done, 1)

            def experts(t, steps, n, *between):
                between = [started(p) for p in between]
                act.wait_ge(xn_ready, t + 1)
                if n == P:
                    act.activation(xn_cur[:, :], xn_next[:, :], ACT.Copy).then_inc(xn_copied, 1)
                else:
                    for q in range(QUADS):
                        act.activation(xn_cur[q * DEC:(q + 1) * DEC, :], xn_next[0:DEC, :],
                                       ACT.Copy).then_inc(xn_copied, 1)
                for s in range(steps // PAIR):
                    k = s * PAIR
                    act.wait_ge(dotted, t * STEPS + k + PAIR)
                    act.activation(dots[:, k:k + PAIR], dots[:, k:k + PAIR],
                                   ACT.Gelu_apprx_tanh).then_inc(gelu_done, 1)
                    for p in between:
                        advance(p, s)
                act.wait_ge(slot_free, RING + t * STEPS + steps)
                act.wait_ge(y_out, 16 * t + 16)
                act.activation(y_sb[0:n, :], expert_sum[0:n, :], ACT.Square,
                               accum_out=stat[0:n, 6:7]).then_inc(sum_squared, 1)
                act.wait_ge(sum_squared, 2 * t + 1)
                act.activation(stat[0:n, 6:7], stat[0:n, 6:7], ACT.Sqrt, bias=eps_sb[0:n, :],
                               scale=1.0 / D).then_inc(sum_squared, 1)

            together(mixer(0, P), projection(GROUP_C), store_conv(GROUP_C))
            projection_stored(act, GROUP_C)
            with act.Fori(0, TILES - 1) as t:
                experts(t, STEPS, P, mixer(t + 1, P))
            experts(TILES - 1, STEPS, P, mixer(TILES, DEC))
            experts(TILES, SAMPLE_STEPS, DEC)

        @block.tensor
        def _(pe):
            pe.wait_ge(normed, 1)
            for k in range(KC):
                pe.wait_ge(squared, 2 * k + 2)
                for (lo, hi), dst in zip(CHUNKS, rms_ps):
                    m = pe.matmul(dst, ones, squares[:, k % 2, lo:hi], start=(k == 0), stop=(k == KC - 1))
                m.then_inc(summed, 1)
            pe.wait_ge(normed, 1 + 2 * KC)

            def projection(g):
                xn = xn_c if g is GROUP_C else xn_a
                for q, (u, kind, i) in enumerate(g.uses):
                    yield g.slot(q)
                    if q == 0:
                        wait(pe, act_took, g.count("act"))
                        wait(pe, dve_took, g.count("dve"))
                    if q >= 2:
                        who, n = g.taken(q - 2)
                        pe.wait_ge(TAKEN[who], g.count(who, n))
                    if q == 0 or u != g.uses[q - 1][0]:
                        pe.wait_ge(unit_in[u % g.buffers], unit_count(g, u))
                    if kind == "tile":
                        w = units[u % g.buffers].rearrange("p (k n) -> p k n", k=KC)
                        m = g.tiles[i]
                        for k in range(KC):
                            ins = pe.matmul(bank[q % 2][0:m, 0:UNIT], xn[:, k, i * P:i * P + m], w[:, k, :],
                                            start=(k == 0), stop=(k == KC - 1))
                    else:
                        w = units[u % g.buffers][:, 0:KC * P].rearrange("p (k n) -> p k n", k=KC)
                        lo, hi = g.chunks[i]
                        for k in range(KC):
                            ins = pe.matmul(bank[q % 2][:, 0:hi - lo], w[:, k, :], xn[:, k, lo:hi],
                                            start=(k == 0), stop=(k == KC - 1))
                    ins.then_inc(projected, 1)

            together(projection(GROUP_A))
            pe.wait_ge(consts_in, 16 * len(CONSTS))
            pe.wait_ge(resident_in, 16 * WQ_RES)

            def mixer(t, n):
                yield S_QKT
                pe.wait_ge(rotated, t + 1)
                for i in range(2):
                    for h in range(H):
                        ins = pe.transpose(tp[:, i, h * P:h * P + n], rot[0:n, i * H + h, :], ident_sb[0:n, 0:n])
                    ins.then_inc(qkT_ready, 1)
                yield S_SCORES
                pe.wait_ge(qkT_copied, t * 2 + 2)
                for h in range(H):
                    ins = pe.matmul(mm[0:n, 0, h * P:h * P + n], qkT[:, H + h, 0:n], qkT[:, h, 0:n],
                                    start=True, stop=True)
                ins.then_inc(scores_ready, 1)
                yield S_OUT
                pe.wait_ge(decayed_ready, t + 1)
                for h in range(H):
                    v = qkvg[0:n, 2 * RET + h * P:2 * RET + (h + 1) * P]
                    pe.matmul(mm[0:n, 1, h * P:(h + 1) * P], decayed[0:n, h, 0:n], v, start=True, stop=True)
                    pe.matmul(tp[0:n, 0, h * P:(h + 1) * P], qkT[:, h, 0:n], state[:, h, :], start=True, stop=True)
                    ins = pe.matmul(tp[:, 1, h * P:(h + 1) * P], k_dec[0:n, h, :], v, start=True, stop=True)
                ins.then_inc(ret_ready, 1)
                yield S_GATEDT
                pe.wait_ge(gated, t + 1)
                for h in range(H):
                    ins = pe.transpose(mm[:, 0, h * P:h * P + n], ret_o[0:n, h, :], ident_sb[0:n, 0:n])
                ins.then_inc(gatedT_ready, 1)
                for k in range(KC):
                    yield S_WOUT + k
                    if k == 0:
                        pe.wait_ge(gatedT_copied, t + 1)
                    for j in range(2):
                        ins = pe.matmul(x1_ps[0:n, j * 512:(j + 1) * 512], catT[:, k, 0:n],
                                        w_out_sb[:, k, j * 512:(j + 1) * 512], start=(k == 0), stop=(k == KC - 1))
                    ins.then_inc(wout_chunk, 1)
                yield S_XNT
                pe.wait_ge(xn_ready, t + 1)
                for i in range(2):
                    if i:
                        yield S_XNT + 1
                    for j in range(4):
                        k = 4 * i + j
                        ins = pe.transpose(tp[:, i, j * P:j * P + n], xn_next[0:n, k * P:(k + 1) * P],
                                           ident_sb[0:n, 0:n])
                    ins.then_inc(xnT_ready, 1)
                def w_of(b):
                    return wq_sb[:, b if b < WQ_RES else WQ_RES + (b - WQ_RES) % WBUF]

                for b in range(BLK + 1):
                    yield S_QUERY + b
                    g, j = divmod(b, 4)
                    if j == 0 and g > 0:
                        pe.wait_ge(query_copied, t * 4 + g)
                        if g >= 3:
                            pe.wait_ge(keyed_copied, t * 4 + g - 2)
                        for i in range(4):
                            ins = pe.matmul(tp[0:n, (g - 1) % 2, i * NK:(i + 1) * NK], qT[:, (g - 1) % 2, i, 0:n],
                                            keys_sb[:, 4 * (g - 1) + i, :], start=True, stop=True)
                        ins.then_inc(keyed, 1)
                    if b == BLK:
                        break
                    if b == 0:
                        pe.wait_ge(xnT_copied, t * 2 + 2)
                    if j == 0 and g >= 2:
                        pe.wait_ge(query_copied, t * 4 + g - 1)
                    if b >= WQ_RES:
                        i = b - WQ_RES
                        pe.wait_ge(wbuf_in[i % WBUF], t * (16 * STREAMED // WBUF) + (i // WBUF + 1) * 16)
                    for k in range(KC):
                        ins = pe.matmul(mm[:, g % 2, j * P:j * P + n], w_of(b)[:, k, :], xnT[:, k, 0:n],
                                        start=(k == 0), stop=(k == KC - 1))
                    ins.then_inc(query_blk, 1)

            def experts(t, steps, n, *between):
                between = [started(p) for p in between]
                pe.wait_ge(xn_ready, t + 1)
                pe.wait_ge(y_ready, t + 1)
                for j in range(2):
                    ins = pe.matmul(expert_sum[0:n, j * 512:(j + 1) * 512], ident_sb[0:n, 0:n],
                                    x1_next[0:n, j * 512:(j + 1) * 512], start=True, stop=False,
                                    skip_group_check=True)
                ins.then_inc(sum_started, 1)
                for s in range(steps // PAIR):
                    pe.wait_ge(diag_ready, t * SLOTS + s + 1)
                    for i in range(PAIR):
                        k = s * PAIR + i
                        for j in range(2):
                            ins = pe.matmul(expert_sum[0:n, j * 512:(j + 1) * 512], diag[:, s % 2, i, 0:n],
                                            ring[:, k % RING, D + j * 512:D + (j + 1) * 512],
                                            start=False, stop=(k == steps - 1), skip_group_check=True)
                        ins.then_inc(slot_free, 1)
                    for p in between:
                        advance(p, s)

            together(mixer(0, P), projection(GROUP_C))
            pe.wait_ge(act_took, GROUP_C.end("act"))
            pe.wait_ge(dve_took, GROUP_C.end("dve"))
            pe.wait_ge(conv_out_done, 16 * GROUP_C.end("blocks"))
            pe.sem_inc(slot_free, RING)
            with pe.Fori(0, TILES - 1) as t:
                experts(t, STEPS, P, mixer(t + 1, P))
            experts(TILES - 1, STEPS, P, mixer(TILES, DEC))
            experts(TILES, SAMPLE_STEPS, DEC)

        @block.vector
        def _(dve):
            dve.sem_inc(y_ready, 1)
            dve.memset(ones, 1.0).then_inc(normed, 1)
            dve.memset(eps_sb[:, :], EPS).then_inc(inits, 1)
            dve.memset(state[:, :, :], 0.0).then_inc(inits, 1)
            dve.memset(new_tail[:, :, 0, :], 0.0).then_inc(inits, 1)
            dve.wait_ge(rooted, len(CHUNKS))
            dve.reciprocal(rstd_all[:, :], rstd_all[:, :]).then_inc(inits, 1)
            dve.wait_ge(inits, 4)
            dve.wait_ge(g_mix_in, 16)
            for k in range(KC):
                dve.scalar_tensor_tensor(xn_a[:, k, :], xn_a[:, k, :], g_mix_sb[:, k:k + 1], rstd_all[:, 0:TOK_A],
                                         ALU.mult, ALU.mult).then_inc(normed, 1)
            for k in range(KC):
                dve.scalar_tensor_tensor(xn_c[:, k, :], xn_c[:, k, :], g_mix_sb[:, k:k + 1], rstd_all[:, TOK_A:],
                                         ALU.mult, ALU.mult).then_inc(normed, 1)

            def projection(g):
                length = g.prompt + (2 + DEC if g.sample else 0)

                def pieces(lo, hi):
                    if not g.sample or hi <= g.prompt:
                        return [(lo, hi, 0)]
                    return [(lo, g.prompt, 0), (g.prompt, hi, 2)]

                for j in range(CH):
                    done = j * g.block_ops
                    at = {kind: [q for q, use in enumerate(g.uses) if use[:2] == (3 * j + i, kind)]
                          for i, kind in enumerate("ChB")}
                    yield g.slot(at["h"][0])
                    if j == 0:
                        dve.wait_ge(par_in, 16)
                        wait(dve, conv_ops, g.count("ops"))
                    dve.tensor_copy(taps[:, 0:2], new_tail[:, j, 0, :]).then_inc(conv_ops, 1)
                    done += 1
                    if g.sample:
                        dve.tensor_copy(taps[:, g.prompt + 2:g.prompt + 4], par[:, j, 3:5]).then_inc(conv_ops, 1)
                        done += 1
                    for (lo, hi), q, qc in zip(g.chunks, at["h"], at["C"]):
                        yield g.slot(q)
                        dve.wait_ge(projected, g.count("uses", q + 1))
                        dve.wait_ge(act_took, g.count("act", g.taken(qc)[1]))
                        for a, b, shift in pieces(lo, hi):
                            ins = dve.tensor_tensor(taps[:, 2 + a + shift:2 + b + shift],
                                                    bank[q % 2][:, a - lo:b - lo], gate_c[:, a:b], ALU.mult)
                            if b < hi:
                                ins.then_inc(conv_ops, 1)
                                done += 1
                        ins.then_inc(dve_took, 1)
                    dve.wait_ge(conv_ops, g.count("ops", done))
                    dve.wait_ge(dve_took, g.count("dve", g.taken(at["h"][-1])[1]))
                    for i in range(3):
                        w = par[:, j, i:i + 1]
                        if i == 0:
                            dve.tensor_scalar(conv_y[:, 0:length], taps[:, 0:length], w, None,
                                              ALU.mult).then_inc(conv_ops, 1)
                        else:
                            dve.scalar_tensor_tensor(conv_y[:, 0:length], taps[:, i:i + length], w,
                                                     conv_y[:, 0:length], ALU.mult, ALU.add).then_inc(conv_ops, 1)
                        done += 1
                        dve.wait_ge(conv_ops, g.count("ops", done))
                    dve.tensor_copy(new_tail[:, j, 0, :], taps[:, g.prompt:g.prompt + 2]).then_inc(conv_ops, 1)
                    done += 1
                    if g.sample:
                        dve.tensor_copy(new_tail[:, j, 1, :], taps[:, length:length + 2]).then_inc(conv_ops, 1)
                        done += 1
                    for (lo, hi), q in zip(g.chunks, at["B"]):
                        yield g.slot(q)
                        dve.wait_ge(projected, g.count("uses", q + 1))
                        if lo == 0:
                            wait(dve, conv_out_done, 16 * (g.count("blocks") + j))
                        for a, b, shift in pieces(lo, hi):
                            ins = dve.tensor_tensor(conv_out[:, a:b], bank[q % 2][:, a - lo:b - lo],
                                                    conv_y[:, a + shift:b + shift], ALU.mult)
                            if b < hi:
                                ins.then_inc(conv_ops, 1)
                                done += 1
                        ins.then_inc(dve_took, 1)
                    assert done == (j + 1) * g.block_ops, (done, g.block_ops)

            together(projection(GROUP_A))

            def mixer(t, n):
                done = [0]

                def op(ins):
                    ins.then_inc(mix_dve, 1)
                    done[0] += 1

                def settle(apart=False):
                    (wait_apart if apart else wait)(dve, mix_dve, t * MIX_OPS + done[0])

                edge = edge_p_sb if n == P else edge_s_sb
                decay = decay_p_sb if n == P else decay_s_sb
                cd = block_decay[0 if n == P else 1]
                yield S_ROPE
                dve.wait_ge(tile_in, 64 * (t + 1))
                qk = qkvg[0:n, 0:2 * RET].rearrange("p (g c) -> p g c", g=2 * H)
                half = P // 2
                op(dve.tensor_tensor(rot[0:n], qk, bc(cs_sb[0:n, 0, :], 1, 2 * H), ALU.mult))
                op(dve.tensor_tensor(swap[0:n, :, 0:half], qk[:, :, half:P],
                                     bc(cs_sb[0:n, 1, 0:half], 1, 2 * H), ALU.mult))
                yield S_ROPE + 1
                op(dve.tensor_tensor(swap[0:n, :, half:P], qk[:, :, 0:half],
                                     bc(cs_sb[0:n, 1, half:P], 1, 2 * H), ALU.mult))
                settle()
                dve.tensor_tensor(rot[0:n], rot[0:n], swap[0:n], ALU.add).then_inc(rotated, 1)
                yield S_KDECAY
                dve.wait_ge(rotated, t + 1)
                op(dve.tensor_tensor(k_dec[0:n], rot[0:n, H:, :], bc(edge[0:n, 1, :], 2, P), ALU.mult))
                yield S_DECAYED
                dve.wait_ge(scores_ready, t + 1)
                settle()
                if n == P:
                    dve.tensor_tensor(decayed[:, :, :], mm[:, 0, :].rearrange("p (h c) -> p h c", h=H),
                                      decay[:, :, :], ALU.mult).then_inc(decayed_ready, 1)
                else:
                    dve.wait_ge(state_out, 32)
                    dve.tensor_tensor(decayed[0:n, :, 0:n],
                                      mm[0:n, 0, :].rearrange("p (h c) -> p h c", h=H)[:, :, 0:n],
                                      decay[:, :, :], ALU.mult).then_inc(decayed_ready, 1)
                yield S_GATED
                dve.wait_ge(ret_ready, t + 1)
                o = ret_o[0:n]
                op(dve.tensor_tensor(o, tp[0:n, 0, :].rearrange("p (h c) -> p h c", h=H),
                                     bc(edge[0:n, 0, :], 2, P), ALU.mult))
                for h in range(H):
                    op(dve.scalar_tensor_tensor(state[:, h, :], state[:, h, :], cd[h],
                                                tp[:, 1, h * P:(h + 1) * P], ALU.mult, ALU.add))
                settle()
                op(dve.tensor_tensor(o, o, mm[0:n, 1, :].rearrange("p (h c) -> p h c", h=H), ALU.add))
                settle()
                yield S_GATED + 1
                sq = ret_sq[0:n]
                op(dve.tensor_tensor(sq, o, o, ALU.mult))
                settle()
                dve.tensor_reduce(stat[0:n, 0:H], sq, AX_X, ALU.add).then_inc(ret_squared, 1)
                yield S_GATED + 2
                dve.wait_ge(ret_rooted, t + 1)
                op(dve.reciprocal(stat[0:n, 0:H], stat[0:n, 0:H]))
                settle()
                op(dve.tensor_tensor(o, o, bc(stat[0:n, 0:H], 2, P), ALU.mult))
                settle()
                dve.wait_ge(silu_done, t + 1)
                dve.tensor_tensor(o, o, qkvg[0:n, 3 * RET:].rearrange("p (h c) -> p h c", h=H),
                                  ALU.mult).then_inc(gated, 1)
                yield S_X1
                dve.wait_ge(wout_chunk, (t + 1) * KC)
                dve.tensor_tensor(x1_next[0:n, :], x1_next[0:n, :], x1_ps[0:n, :], ALU.add).then_inc(x1_ready, 1)
                yield S_XN
                dve.wait_ge(x1_squared, 2 * t + 2)
                op(dve.reciprocal(stat[0:n, 5:6], stat[0:n, 4:5]))
                settle()
                dve.scalar_tensor_tensor(xn_next[0:n, :], x1_next[0:n, :], stat[0:n, 5:6], g_ffn_sb[0:n, :],
                                         ALU.mult, ALU.mult).then_inc(xn_ready, 1)
                for b in range(BLK):
                    yield S_TOP + b
                    if b % 4 == 0:
                        wait_apart(dve, keyed_copied, t * 4 + b // 4 + 1)
                    s = scores[0:n, b, :]
                    rest = left[0:n, (b % 2) * NK:(b % 2 + 1) * NK]
                    op(dve.max(top_v[0:n, b, 0:8], s))
                    settle(apart=True)
                    op(dve.max_index(top_i[0:n, b, 0:8], top_v[0:n, b, 0:8], s))
                    op(dve.match_replace(rest, top_v[0:n, b, 0:8], s, LOWEST))
                    settle(apart=True)
                    op(dve.max(top_v[0:n, b, 8:16], rest))
                    settle(apart=True)
                    op(dve.max_index(top_i[0:n, b, 8:16], top_v[0:n, b, 8:16], rest))
                yield S_PAIRS
                settle()
                tv = top_v[0:n].rearrange("p (h s) k -> p h s k", s=2)
                shape = [n, PH, TOPK, TOPK]
                op(dve.tensor_tensor(pairs[0:n], tv[:, :, 0, :].unsqueeze(3).broadcast_to(shape),
                                     tv[:, :, 1, :].unsqueeze(2).broadcast_to(shape), ALU.add))
                op(dve.tensor_copy(top_f[0:n], top_i[0:n]))
                settle()
                for h in range(PH):
                    yield S_BEST + h
                    s = pairs[0:n, h].rearrange("p i j -> p (i j)")
                    rest = left[0:n, :]
                    op(dve.max(best_v[0:n, h, 0:8], s))
                    settle(apart=True)
                    op(dve.max_index(best_i[0:n, h, 0:8], best_v[0:n, h, 0:8], s))
                    op(dve.match_replace(rest, best_v[0:n, h, 0:8], s, LOWEST))
                    settle(apart=True)
                    op(dve.max(best_v[0:n, h, 8:16], rest))
                    settle(apart=True)
                    op(dve.max_index(best_i[0:n, h, 8:16], best_v[0:n, h, 8:16], rest))
                    settle(apart=True)
                yield S_PICK
                wait(dve, gate_copied, t)
                dve.tensor_tensor(gate_next[0:n], best_v[0:n], best_v[0:n, :, 0:1].broadcast_to([n, PH, TOPK]),
                                  ALU.subtract).then_inc(exp_in, 1)
                flat_i = best_i[0:n].rearrange("p h k -> p (h k)")
                op(dve.tensor_single_scalar(half_i[0:n, 0, :], flat_i, 4, ALU.logical_shift_right))
                op(dve.tensor_single_scalar(half_i[0:n, 1, :], flat_i, 15, ALU.bitwise_and))
                settle()
                op(dve.tensor_copy(half_f[0:n], half_i[0:n]))
                settle()
                tf = top_f[0:n].rearrange("p (h s) k -> p h s k", s=2)
                hot = onehot[0:n]
                for s in range(2):
                    yield S_PICK + 1 + 2 * s
                    op(dve.tensor_tensor(hot, bc(iota_sb[0:n, :], 1, STEPS), bc(half_f[0:n, s, :], 2, TOPK),
                                         ALU.is_equal))
                    settle()
                    yield S_PICK + 2 + 2 * s
                    hot4 = hot.rearrange("p (h k) j -> p h k j", h=PH)
                    op(dve.tensor_tensor(hot4, hot4, tf[:, :, s, :].unsqueeze(2).broadcast_to(shape), ALU.mult))
                    settle()
                    op(dve.tensor_reduce(pick_f[0:n, s, :], hot, AX_X, ALU.add))
                    settle()
                yield S_PICK + 5
                dve.wait_ge(exp_done, t + 1)
                op(dve.tensor_reduce(reduced[0:n, 0:PH], gate_next[0:n], AX_X, ALU.add))
                settle()
                op(dve.reciprocal(reduced[0:n, PH:], reduced[0:n, 0:PH]))
                settle()
                op(dve.tensor_tensor(gate_next[0:n], gate_next[0:n], bc(reduced[0:n, PH:], 2, TOPK), ALU.mult))
                settle()
                wait(dve, idx_copied, 2 * t)
                dve.scalar_tensor_tensor(idx_next[0:n, :], pick_f[0:n, 0, :], float(NK), pick_f[0:n, 1, :],
                                         ALU.mult, ALU.add).then_inc(chosen, 1)
                assert done[0] == MIX_OPS, done[0]

            def experts(t, steps, n, *between):
                between = [started(p) for p in between]
                dve.wait_ge(chosen, t + 1)
                if n == P:
                    dve.tensor_copy(gate_cur[:, :], gate_next[:].rearrange("p h k -> p (h k)")).then_inc(gate_copied, 1)
                else:
                    gates = gate_next[:].rearrange("p h k -> p (h k)")
                    for q in range(QUADS):
                        rows, cols = slice(q * DEC, (q + 1) * DEC), slice(q * steps, (q + 1) * steps)
                        dve.tensor_copy(idx_cur[rows, 0:steps], idx_next[0:DEC, cols]).then_inc(idx_copied, 1)
                        dve.tensor_copy(gate_cur[rows, 0:steps], gates[0:DEC, cols]).then_inc(gate_copied, 1)
                copies = 1 if n == P else QUADS
                dve.wait_ge(gate_copied, t + copies)
                dve.wait_ge(xn_copied, t + copies)
                for s in range(steps // PAIR):
                    for i in range(PAIR):
                        k = s * PAIR + i
                        dve.wait_ge(landed[k % RING], t * 16 * (STEPS // RING) + 16 * (k // RING + 1))
                        u = ring[:, k % RING, 0:D]
                        dve.tensor_tensor_reduce(u, u, xn_cur[:, :], 1.0, 0.0, ALU.mult, ALU.add,
                                                 dots[:, k:k + 1]).then_inc(dotted, 1)
                    k = s * PAIR
                    dve.wait_ge(gelu_done, t * SLOTS + s + 1)
                    dve.tensor_tensor(weights[:, k:k + PAIR], dots[:, k:k + PAIR], gate_cur[:, k:k + PAIR],
                                      ALU.mult).then_inc(weighed, 1)
                    dve.wait_ge(weighed, t * SLOTS + s + 1)
                    eye = ident_sb if n == P else sel_sb
                    dve.wait_ge(slot_free, t * STEPS + (s - 1) * PAIR + RING)
                    dve.tensor_tensor(diag[:, s % 2, :, 0:n], bc(eye[:, 0:n], 1, PAIR),
                                      bc(weights[:, k:k + PAIR], 2, n), ALU.mult).then_inc(diag_ready, 1)
                    for p in between:
                        advance(p, s)
                dve.wait_ge(sum_squared, 2 * t + 2)
                dve.reciprocal(stat[0:n, 7:8], stat[0:n, 6:7]).then_inc(sum_stat, 1)
                dve.wait_ge(sum_stat, t + 1)
                dve.scalar_tensor_tensor(y_sb[0:n, :], expert_sum[0:n, :], stat[0:n, 7:8], g_fin_sb[0:n, :],
                                         ALU.mult, ALU.mult).then_inc(y_ready, 1)

            dve.wait_ge(consts_in, 16 * len(CONSTS))
            together(mixer(0, P), projection(GROUP_C))
            with dve.Fori(0, TILES - 1) as t:
                experts(t, STEPS, P, mixer(t + 1, P))
            experts(TILES - 1, STEPS, P, mixer(TILES, DEC))
            experts(TILES, SAMPLE_STEPS, DEC)


_OUTS = [("y", (TOK, D)), ("ret_p", (P, H, P)), ("ret_s", (P, H, P)), ("conv_p", (P, CH, 2)), ("conv_s", (P, CH, 2))]


def constants():
    import numpy as np

    f = np.float32
    half = P // 2
    inv = np.power(f(10000.0), -np.arange(half, dtype=f) / f(half)).astype(f)
    angle = (np.arange(TOK, dtype=f)[:, None] * inv[None, :]).astype(f)
    cos, sin = np.cos(angle).astype(f), np.sin(angle).astype(f)
    cos_sin = np.stack([np.concatenate([cos, cos], 1), np.concatenate([-sin, sin], 1)], 1)
    lg = np.log1p(-np.exp2(-5.0 - np.arange(H))).astype(f).astype(np.float64)
    scale = P ** -0.5

    def tables(n, chunk):
        i = np.arange(n)
        seen = (i[:, None] // chunk) <= (i[None, :] // chunk)
        decay = np.exp(lg[None, :, None] * np.abs(i[:, None] - i[None, :])[:, None, :]) * seen[:, None, :] * scale
        edge = np.stack([np.exp(lg[None, :] * (i[:, None] + 1.0)) * scale,
                         np.exp(lg[None, :] * (n - 1.0 - i[:, None]))], 1)
        return decay.astype(f), edge.astype(f), [float(v) for v in np.exp(lg * n)]

    dp, ep, cp = tables(P, 64)
    ds, es, cs = tables(DEC, DEC)
    eye = np.eye(P, dtype=f)
    sel = np.tile(np.eye(DEC, dtype=f), (QUADS, 1))
    iota = np.tile(np.arange(TOPK, dtype=f), (P, 1))
    return dict(cos_sin=cos_sin, decay_p=dp, decay_s=ds, edge_p=ep, edge_s=es, ident=eye, sel=sel, iota=iota), (cp, cs)


def kernel(x_prompt, x_sample, state_ret, state_conv, norm_mix_g, w_in, conv_w, w_out, norm_ffn_g, peer_wq,
           peer_keys1, peer_keys2, peer_u, peer_v, norm_final_g):
    import numpy as np
    import concourse.bacc as bacc
    from concourse.bass_utils import run_bass_kernel_spmd as run

    a = np.asarray
    x = np.concatenate([a(x_prompt)[0], a(x_sample)[0]], 0)
    w = a(w_in)[0]
    by_chunk = w.reshape(KC, P, -1)
    w_ret = by_chunk[:, :, 0:4 * RET].reshape(KC, P, -1, UNIT).transpose(2, 1, 0, 3).reshape(-1, P, KC * UNIT)
    b_c_h = by_chunk[:, :, 4 * RET:].reshape(KC, P, 3, CH, P)[:, :, [1, 2, 0]]
    w_conv = b_c_h.transpose(3, 2, 1, 0, 4).reshape(3 * CH, P, KC * P)
    keys = np.stack([a(peer_keys1)[0], a(peer_keys2)[0]], 1).reshape(BLK, NK, P)

    def by_channel(v):
        return v.reshape(-1, CH, P).transpose(2, 1, 0)

    consts, block_decay = constants()
    data = dict(
        xT=x.T, x=x, w_ret=w_ret, w_conv=w_conv,
        w_out=a(w_out)[0].reshape(KC, P, D).transpose(1, 0, 2),
        wq=a(peer_wq)[0].reshape(KC, P, BLK, P).transpose(2, 1, 0, 3),
        keysT=keys.transpose(2, 0, 1),
        uv=np.concatenate([a(peer_u)[0], a(peer_v)[0]], 1),
        g_mix=a(norm_mix_g)[0].reshape(KC, P).T,
        g_ffn=np.broadcast_to(a(norm_ffn_g), (P, D)),
        g_fin=np.broadcast_to(a(norm_final_g)[None], (P, D)),
        conv_par=np.concatenate([by_channel(a(conv_w)[0]), by_channel(a(state_conv)[0, 0])], 2),
        ret_state=a(state_ret)[0, 0].transpose(1, 0, 2),
        **consts,
    )
    nc = bacc.Bacc("TRN2", target_bir_lowering=False, num_devices=1)
    arrays, aps = {}, {}
    for name, v in data.items():
        v = np.ascontiguousarray(v)
        arrays[f"in_{name}"] = v
        aps[name] = nc.dram_tensor(f"in_{name}", v.shape, mybir.dt.from_np(v.dtype), kind="ExternalInput").ap()
    outs = [nc.dram_tensor(f"out_{n}", s, F32, kind="ExternalOutput").ap() for n, s in _OUTS]
    layer_kernel(nc, **aps, block_decay=block_decay, y=outs[0], out_ret_p=outs[1], out_ret_s=outs[2],
                 out_conv_p=outs[3], out_conv_s=outs[4])
    r = run(nc, [arrays], core_ids=[0]).results[0]
    y = r["out_y"]

    def ret(v):
        return v.transpose(1, 0, 2)[None, None]

    def conv(v):
        return v.transpose(2, 1, 0).reshape(1, 1, 2, CH * P)

    return (y[None, :SEQ], y[None, SEQ:], ret(r["out_ret_p"]), conv(r["out_conv_p"]),
            ret(r["out_ret_s"]), conv(r["out_conv_s"]))
```
